# Optimizing a Trainium2 kernel written in Bass

```python
import jax, jax.numpy as jnp
from jax import lax
import numpy as np

D_MODEL = 1024
BATCH = 1
SEQ = 512
DEPTH = 1

PLE_DIM = 256
POOL_GROUPS = 4
POOL_GROUP_DIM = 128
POOL_WINDOWS = (2, 4, 8, 16)
POOL_DIM = POOL_GROUPS * POOL_GROUP_DIM
N_HEADS = 8
N_KV_HEADS = 2
HEAD_DIM = 64
Q_GROUP = N_HEADS // N_KV_HEADS
Q_DIM = N_HEADS * HEAD_DIM
KV_DIM = N_KV_HEADS * HEAD_DIM
WINDOW = 128
ATTN_BLOCK = 128
IN_DIM = POOL_DIM + Q_DIM + 2 * KV_DIM
N_EXPERTS = 64
N_EXPERT_GROUPS = 8
TOPK_GROUPS = 4
TOP_K = 8
EXPERT_DIM = 256
SHARED_DIM = 256
ROUTED_SCALE = 2.5
MOE_BLOCK = 256
EPS = 1e-6

kernel_name = "hybrid_pool_swa_moe_block"

def rmsnorm(x, g):
    xf = x.astype(jnp.float32)
    xf = xf * lax.rsqrt(jnp.mean(xf * xf, axis=-1, keepdims=True) + EPS)
    return xf.astype(x.dtype) * g

def alibi_slopes(n_heads):
    return jnp.asarray(2.0 ** (-8.0 * (np.arange(n_heads) + 1) / n_heads), dtype=jnp.float32)

def pool_mixer(u, w_mix, scale):
    B, S, _ = u.shape
    uf = u.astype(jnp.float32).reshape(B, S, POOL_GROUPS, POOL_GROUP_DIM)
    cs = jnp.concatenate([jnp.zeros((B, 1, POOL_GROUPS, POOL_GROUP_DIM), jnp.float32),
                          jnp.cumsum(uf, axis=1)], axis=1)
    t = jnp.arange(S)
    outs = []
    for g, w in enumerate(POOL_WINDOWS):
        lo = jnp.maximum(t + 1 - w, 0)
        window_sum = cs[:, 1:, g] - cs[:, lo, g]
        count = jnp.minimum(t + 1, w).astype(jnp.float32)[None, :, None]
        outs.append(window_sum / count - uf[:, :, g])
    pooled = jnp.stack(outs, axis=2).astype(u.dtype)
    mixed = jnp.einsum('bsgc,gcd->bsgd', pooled, w_mix)
    return mixed.reshape(B, S, POOL_DIM) * scale

def swa_attention(q, k, v, q_gain, k_gain, sinks):
    B, S, _ = q.shape
    nb = S // ATTN_BLOCK
    q = rmsnorm(q.reshape(B, S, N_HEADS, HEAD_DIM), q_gain)
    k = rmsnorm(k.reshape(B, S, N_KV_HEADS, HEAD_DIM), k_gain)
    v = v.reshape(B, S, N_KV_HEADS, HEAD_DIM)
    qb = q.reshape(B, nb, ATTN_BLOCK, N_KV_HEADS, Q_GROUP, HEAD_DIM).astype(jnp.float32)

    def band(t):
        tb = t.reshape(B, nb, ATTN_BLOCK, N_KV_HEADS, HEAD_DIM)
        prev = jnp.concatenate([jnp.zeros_like(tb[:, :1]), tb[:, :-1]], axis=1)
        return jnp.concatenate([prev, tb], axis=2).astype(jnp.float32)

    kw, vw = band(k), band(v)
    scores = jnp.einsum('bnqkgd,bnskd->bnkgqs', qb, kw) * (HEAD_DIM ** -0.5)
    i = jnp.arange(ATTN_BLOCK)[:, None]
    j = jnp.arange(2 * ATTN_BLOCK)[None, :]
    dist = (ATTN_BLOCK + i - j)
    in_window = (dist >= 0) & (dist < WINDOW)
    key_exists = (jnp.arange(nb)[:, None] > 0) | (jnp.arange(2 * ATTN_BLOCK)[None, :] >= ATTN_BLOCK)
    mask = in_window[None] & key_exists[:, None, :]
    slopes = alibi_slopes(N_HEADS).reshape(N_KV_HEADS, Q_GROUP)
    scores = scores - slopes[:, :, None, None] * dist.astype(jnp.float32)
    scores = jnp.where(mask[None, :, None, None], scores, -jnp.inf)
    sink = sinks.astype(jnp.float32).reshape(N_KV_HEADS, Q_GROUP)[None, None, :, :, None, None]
    m = jnp.maximum(jnp.max(scores, axis=-1, keepdims=True), sink)
    e = jnp.exp(scores - m)
    probs = e / (jnp.sum(e, axis=-1, keepdims=True) + jnp.exp(sink - m))
    out = jnp.einsum('bnkgqs,bnskd->bnqkgd', probs, vw)
    return out.reshape(B, S, Q_DIM).astype(q.dtype)

def swiglu(x, wg, wu, wd):
    return (jax.nn.silu(x @ wg) * (x @ wu)) @ wd

def route(h, w_router, bias):
    T = h.shape[0]
    scores = jax.nn.sigmoid(h.astype(jnp.float32) @ w_router.astype(jnp.float32))
    choice = scores + bias.astype(jnp.float32)
    grp = choice.reshape(T, N_EXPERT_GROUPS, N_EXPERTS // N_EXPERT_GROUPS)
    grp_score = lax.top_k(grp, 2)[0].sum(-1)
    _, top_groups = lax.top_k(grp_score, TOPK_GROUPS)
    gmask = jax.nn.one_hot(top_groups, N_EXPERT_GROUPS, dtype=jnp.float32).sum(1) > 0
    emask = jnp.repeat(gmask, N_EXPERTS // N_EXPERT_GROUPS, axis=1)
    _, idx = lax.top_k(jnp.where(emask, choice, -jnp.inf), TOP_K)
    w = jnp.take_along_axis(scores, idx, axis=1)
    w = w / (jnp.sum(w, axis=-1, keepdims=True) + 1e-20) * ROUTED_SCALE
    return idx, w

def routed_experts(h, idx, w, w_gate, w_up, w_down):
    T, D = h.shape
    A = T * TOP_K
    e_flat = idx.reshape(A).astype(jnp.int32)
    tok_flat = (jnp.arange(A, dtype=jnp.int32) // TOP_K)
    w_flat = w.reshape(A)
    order = jnp.argsort(e_flat)
    e_sorted = e_flat[order]
    counts = jnp.bincount(e_flat, length=N_EXPERTS).astype(jnp.int32)
    start = jnp.cumsum(counts) - counts
    padded = (counts + MOE_BLOCK - 1) // MOE_BLOCK * MOE_BLOCK
    pend = jnp.cumsum(padded)
    pstart = pend - padded
    dest = pstart[e_sorted] + (jnp.arange(A, dtype=jnp.int32) - start[e_sorted])
    n_blocks = -(-A // MOE_BLOCK) + N_EXPERTS
    P = n_blocks * MOE_BLOCK
    tok_buf = jnp.full((P,), T, jnp.int32).at[dest].set(tok_flat[order])
    w_buf = jnp.zeros((P,), jnp.float32).at[dest].set(w_flat[order])
    block_e = jnp.minimum(jnp.searchsorted(pend, jnp.arange(n_blocks, dtype=jnp.int32) * MOE_BLOCK,
                                           side='right'), N_EXPERTS - 1)
    h_pad = jnp.concatenate([h, jnp.zeros((1, D), h.dtype)], axis=0)

    def body(acc, xs):
        tok, wt, e = xs
        y = swiglu(h_pad[tok], w_gate[e], w_up[e], w_down[e])
        return acc.at[tok].add(y.astype(jnp.float32) * wt[:, None]), None

    acc, _ = lax.scan(body, jnp.zeros((T + 1, D), jnp.float32),
                      (tok_buf.reshape(n_blocks, MOE_BLOCK), w_buf.reshape(n_blocks, MOE_BLOCK), block_e))
    return acc[:T].astype(h.dtype)

def setup_inputs(seed: int = 0) -> dict:
    key = jax.random.key(seed)
    ks = jax.random.split(key, 32)
    f32 = jnp.float32
    L, D = DEPTH, D_MODEL

    def nrm(k, shape, fan_in):
        return jax.random.normal(k, shape, f32) * (fan_in ** -0.5)

    def gain(k, shape):
        return 1.0 + 0.05 * jax.random.normal(k, shape, f32)

    return {
        "x": jax.random.normal(ks[0], (BATCH, SEQ, D), f32),
        "p": jax.random.normal(ks[1], (DEPTH, BATCH, SEQ, PLE_DIM), f32),
        "g_mix": gain(ks[2], (L, D)),
        "w_in": nrm(ks[3], (L, D, IN_DIM), D),
        "w_pool_mix": nrm(ks[4], (L, POOL_GROUPS, POOL_GROUP_DIM, POOL_GROUP_DIM), POOL_GROUP_DIM),
        "pool_scale": gain(ks[5], (L, POOL_DIM)),
        "w_branch_a": nrm(ks[6], (L, POOL_DIM, D), POOL_DIM),
        "q_gain": gain(ks[7], (L, HEAD_DIM)),
        "k_gain": gain(ks[8], (L, HEAD_DIM)),
        "attn_sinks": 0.5 * jax.random.normal(ks[9], (L, N_HEADS), f32),
        "w_branch_b": nrm(ks[10], (L, Q_DIM, D), Q_DIM),
        "w_gate": nrm(ks[11], (L, D, 2 * D), D),
        "b_gate": 0.1 * jax.random.normal(ks[12], (L, 2 * D), f32),
        "w_out": nrm(ks[13], (L, D, D), D),
        "g_ffn": gain(ks[14], (L, D)),
        "w_router": nrm(ks[15], (L, D, N_EXPERTS), D),
        "router_bias": 0.01 * jax.random.normal(ks[16], (L, N_EXPERTS), f32),
        "w_exp_gate": nrm(ks[17], (L, N_EXPERTS, D, EXPERT_DIM), D),
        "w_exp_up": nrm(ks[18], (L, N_EXPERTS, D, EXPERT_DIM), D),
        "w_exp_down": nrm(ks[19], (L, N_EXPERTS, EXPERT_DIM, D), EXPERT_DIM),
        "w_sh_gate": nrm(ks[20], (L, D, SHARED_DIM), D),
        "w_sh_up": nrm(ks[21], (L, D, SHARED_DIM), D),
        "w_sh_down": nrm(ks[22], (L, SHARED_DIM, D), SHARED_DIM),
        "g_ple": gain(ks[23], (L, D)),
        "w_ple_gate": nrm(ks[24], (L, D, D), D),
        "w_ple_proj": nrm(ks[25], (L, PLE_DIM, D), PLE_DIM),
        "g_ple_post": gain(ks[26], (L, D)),
    }

def reference(x, p, g_mix, w_in, w_pool_mix, pool_scale, w_branch_a, q_gain, k_gain, attn_sinks,
              w_branch_b, w_gate, b_gate, w_out, g_ffn, w_router, router_bias, w_exp_gate, w_exp_up,
              w_exp_down, w_sh_gate, w_sh_up, w_sh_down, g_ple, w_ple_gate, w_ple_proj, g_ple_post):
    B, S, D = x.shape
    T = B * S
    for i in range(DEPTH):
        h = rmsnorm(x, g_mix[i])
        u = h @ w_in[i]
        u_pool = u[..., :POOL_DIM]
        q = u[..., POOL_DIM:POOL_DIM + Q_DIM]
        k = u[..., POOL_DIM + Q_DIM:POOL_DIM + Q_DIM + KV_DIM]
        v = u[..., POOL_DIM + Q_DIM + KV_DIM:]
        y_a = pool_mixer(u_pool, w_pool_mix[i], pool_scale[i]) @ w_branch_a[i]
        y_b = swa_attention(q, k, v, q_gain[i], k_gain[i], attn_sinks[i]) @ w_branch_b[i]
        gates = jax.nn.sigmoid(h @ w_gate[i] + b_gate[i])
        merged = gates[..., :D] * y_a + gates[..., D:] * y_b
        x = x + merged @ w_out[i]
        h2 = rmsnorm(x, g_ffn[i]).reshape(T, D)
        idx, wts = route(h2, w_router[i], router_bias[i])
        moe = routed_experts(h2, idx, wts, w_exp_gate[i], w_exp_up[i], w_exp_down[i]) \
            + swiglu(h2, w_sh_gate[i], w_sh_up[i], w_sh_down[i])
        x = x + moe.reshape(B, S, D)
        ple_gate = jax.nn.sigmoid(rmsnorm(x, g_ple[i]) @ w_ple_gate[i])
        x = x + ple_gate * rmsnorm(p[i] @ w_ple_proj[i], g_ple_post[i])
    return x


_drawn_inputs = setup_inputs


def setup_inputs(seed=0):
    import zlib

    import numpy as np

    out = dict(_drawn_inputs(seed))
    spreads = {}
    factors = {'g_ple': 8.0, 'g_ple_post': 3.059}
    for name, (base, spread) in spreads.items():
        noise = np.random.default_rng([zlib.crc32(name.encode()), seed]).standard_normal(out[name].shape)
        drawn = base * np.exp(spread * noise) if base else spread * noise
        out[name] = __import__('jax').numpy.asarray(drawn.astype(out[name].dtype))
    for name, factor in factors.items():
        out[name] = (out[name] * factor).astype(out[name].dtype)
    return out
```

```python
from contextlib import ExitStack

import numpy as np

import concourse.bass as bass
from concourse import mybir

ALU = mybir.AluOpType
ACT = mybir.ActivationFunctionType
AX_X = mybir.AxisListType.X
F32 = mybir.dt.float32
BF16 = mybir.dt.bfloat16
U32 = mybir.dt.uint32

P = 128
T = 512
NT = T // P
D = 1024
KD = D // P
POOL_WINDOWS = (2, 4, 8, 16)
NG = len(POOL_WINDOWS)
PAD = 16
NH, NKV, DH = 8, 2, 64
QD, KVD = NH * DH, NKV * DH
WINDOW = 128
PLE = 256
NE, NEG, EPG = 64, 8, 8
TOPG, TOPK = 4, 8
FE = 256
ROUTED_SCALE = 2.5
EPS = 1e-6
BIG = 3.0e38

CAP = 96
DUMP = T
ACC_ROWS = T + P
ROUNDS = -(-T // CAP)

SLOTS = 12
UNIT = 2048
UNROLL = SLOTS // 3
AHEAD = UNROLL - 1
TURNS = NE // UNROLL
NVEC = 22
LCOL = 6
CHUNK = 8

C_ID, C_SLT, C_ONE = 0, P, 2 * P
C_IOTA = 3 * P
C_IOTA8 = C_IOTA + CAP
C_TILE = C_IOTA8 + 8
C_P = C_TILE + NT
C_NDUMP = C_P + 1
C_IC = C_NDUMP + 1
C_ALL = C_IC + NG * PAD


def constant_table():
    c = np.zeros((P, C_ALL), np.float32)
    p = np.arange(P)
    c[:, C_ID:C_ID + P] = np.eye(P)
    c[:, C_SLT:C_SLT + P] = p[:, None] < p[None, :]
    c[:, C_ONE:C_ONE + P] = 1
    c[:, C_IOTA:C_IOTA + CAP] = np.arange(CAP)
    c[:, C_IOTA8:C_IOTA8 + 8] = np.arange(8)
    c[:, C_TILE:C_TILE + NT] = np.arange(NT)
    c[:, C_P] = p
    c[:, C_NDUMP] = -(DUMP + p)
    for g, w in enumerate(POOL_WINDOWS):
        c[:, C_IC + g * PAD:C_IC + (g + 1) * PAD] = 1.0 / np.minimum(np.arange(PAD) + 1, w)
    return c


def head_order():
    return [kv * 4 + 2 * half + par for kv in range(NKV) for par in range(2) for half in range(2)]


def alibi_table():
    i = np.arange(P)[:, None]
    j = np.arange(2 * P)[None, :]
    dist = P + i - j
    ok = (dist >= 0) & (dist < WINDOW)
    slopes = (2.0 ** (-8.0 * (np.arange(NH) + 1) / NH)).astype(np.float32)
    out = np.zeros((P, NH, 2 * P), np.float32)
    for n, h in enumerate(head_order()):
        out[:, n, :] = np.where(ok, -slopes[h] * dist.astype(np.float32), np.float32(-1e30))
    return out.reshape(P, NH * 2 * P)


DENSE = ["q0", "q1", "kv", "pool0", "pool1"] + [f"gate{c}" for c in range(8)] + \
    ["wa0", "wb0", "wa1", "wb1"] + [f"out{c}" for c in range(4)] + ["shg", "shu", "ple", "shd"]
DENSE_SLOT = [u % 8 for u in range(17)] + [1, 2, 3, 4, 5, 6, 7, 8]
DENSE_AT = {name: n for n, name in enumerate(DENSE)}
N_DENSE = len(DENSE)
EXPERT_SLOT = [9, 0, 3, 6]
TAIL_SLOT = [9, 10, 11, 0]


def uses_before(slot, unit):
    return sum(1 for n in range(unit) if DENSE_SLOT[n] == slot)


USES = [uses_before(s, N_DENSE) for s in range(SLOTS)]


def build(nc, t, acc, h2_dram, out):
    ctx = ExitStack()
    with ctx:
        def sb(name, shape, dt=F32):
            return ctx.enter_context(nc.sbuf_tensor(name, shape, dt))

        def sem(name):
            return ctx.enter_context(nc.semaphore(name))

        ring = sb("ring", [P, SLOTS, UNIT])
        xrow = sb("xrow", [P, NT, D])
        actT = sb("actT", [P, KD, T])
        rows = sb("rows", [P, NT, D])
        gates = sb("gates", [P, 2 * KD, T])
        poolbuf = sb("poolbuf", [P, (NG + 2) * (T + PAD)])
        qT = sb("qT", [P, 4, T])
        kT = sb("kT", [P, NKV, T])
        cst = sb("cst", [P, C_ALL])
        mixw = sb("mixw", [P, NG, P])
        vecs = sb("vecs", [NVEC, P])
        vecT = sb("vecT", [P, NVEC])
        gcol = sb("gcol", [P, 2, KD])
        sink_in = sb("sink_in", [P, NH])
        sink = sb("sink", [P, NH])
        st = sb("st", [P, 4, 16])
        mhalf = sb("mhalf", [P, 16])
        smx = sb("smx", [P, 8, NH])
        slot_ix = sb("slot_ix", [P, NE], U32)
        slot_w = sb("slot_w", [P, NE])
        stage = sb("stage", [P, 2, UNROLL, 1], U32)
        maxcnt = sb("maxcnt", [P, 1], U32)
        tickets = sb("tickets", [P, 4])

        bias_t = ring[:, 8, :].rearrange("p (h k) -> p h k", h=NH)
        score = ring[:, 9, :].rearrange("p (h k) -> p h k", h=NH)
        probT = ring[:, 10, :].rearrange("p (b k) -> p b k", b=4)
        pooled = ring[:, 11, :].rearrange("p (g n) -> p g n", g=NG)
        qsq = ring[:, 9, 0:QD + KVD]
        upool = poolbuf[:, 0:NG * (T + PAD)].rearrange("p (g n) -> p g n", g=NG)
        win = [poolbuf[:, (NG + k) * (T + PAD):(NG + k + 1) * (T + PAD)] for k in range(2)]
        mixedT = upool[:, :, PAD:PAD + T]
        gffn = poolbuf[:, 0:D]
        place = poolbuf[:, 0:2 * NT * CHUNK * CAP // 2].bitcast(BF16).rearrange(
            "p (b i e r) -> p b i e r", b=2, i=NT, e=CHUNK)
        sgate = [poolbuf[:, k * D:(k + 1) * D] for k in range(2)]
        lo = gates[:, 0:KD, :].rearrange("p a n -> p (a n)")
        hi = gates[:, KD:2 * KD, :].rearrange("p a n -> p (a n)")
        pp = hi.rearrange("p (i n) -> p i n", i=NT)
        prow = hi[:, 2 * D:3 * D].rearrange("p (i n) -> p i n", i=NT)
        rw = hi[:, 3 * D:3 * D + KD * NE].rearrange("p (k e) -> p k e", k=KD)
        sh_silu = lo[:, 0:2 * T].rearrange("p (j n) -> p j n", j=2)
        sh_act = lo[:, 2 * T:4 * T].rearrange("p (j n) -> p j n", j=2)
        gpost = lo[:, 2 * D:3 * D]
        NR = NT * NE
        r_lt = lo[0:NE, 3 * D:3 * D + T]
        choice = lo[:, 3 * D:3 * D + NR]
        masked = lo[:, 3 * D + NR:3 * D + 2 * NR]
        repl = lo[:, 3 * D + 3 * NR:3 * D + 4 * NR]
        qa = qT[:, :, :].rearrange("p a n -> p (a n)")
        pT = qa[:, 0:1024].rearrange("p (j n) -> p j n", j=2)
        r_sc, r_sel, r_w, r_rank = (qa[:, 1024 + k * NR:1024 + (k + 1) * NR] for k in range(4))
        ka = kT[:, :, :].rearrange("p a n -> p (a n)")
        LM = NR * LCOL // 2
        tokcol = ka[:, 0:LM].bitcast(BF16).rearrange("p (i e c) -> p i e c", i=NT, e=NE)
        selb = ka[:, LM:LM + NR // 2].bitcast(BF16)
        rbias = ka[:, LM + NR // 2:LM + NR // 2 + NE]
        small = ka[:, LM + NR // 2 + NE:2 * T]
        o_place = poolbuf[:, 0:NT * CAP // 2].bitcast(BF16).rearrange("p (i r) -> p i r", i=NT)
        o_iota = sb("o_iota", [P, CAP])
        o_lst = sb("o_lst", [P, LCOL + 4])
        o_ix = sb("o_ix", [P, 1], U32)
        O_SLOT = 3
        triT = sb("triT", [P, P], BF16)
        oneT = sb("oneT", [P, P], BF16)
        hg = [xrow[:, k, :] for k in range(UNROLL)]
        yrow = [rows[:, k, :] for k in range(UNROLL)]
        hgT = [lo[:, k * KD * CAP:(k + 1) * KD * CAP].rearrange("p (k n) -> p k n", k=KD) for k in range(2)]
        eactT = [lo[:, 1536 + k * 2 * CAP:1536 + (k + 1) * 2 * CAP].rearrange("p (j n) -> p j n", j=2)
                 for k in range(2)]
        esilu = [lo[:, 3 * D + k * FE:3 * D + (k + 1) * FE] for k in range(2)]
        eact = [lo[:, 3 * D + (2 + k) * FE:3 * D + (3 + k) * FE] for k in range(2)]
        lists_sb = rows[:, 0, 0:NE * LCOL].rearrange("p (e c) -> p e c", c=LCOL)
        ltmp = [rows[:, 0, 512 + k * NE:512 + (k + 1) * NE] for k in range(4)]

        ps = ctx.enter_context(nc.psum_tensor("ps", [P, 8 * 512], F32))

        def bank(b, n=1):
            return ps[:, b * 512:(b + n) * 512]

        ident = cst[:, C_ID:C_ID + P]

        slot_loaded = [sem(f"slot_loaded{s}") for s in range(SLOTS)]
        x_loaded = [sem(f"x_loaded{i}") for i in range(NT)]
        gmix_loaded = sem("gmix_loaded")
        cst_loaded, small_loaded, bias_loaded = sem("cst_loaded"), sem("small_loaded"), sem("bias_loaded")
        ssq_done, rstd_ready, rows_ready = sem("ssq_done"), sem("rstd_ready"), sem("rows_ready")
        hT_ps, hT_ready = sem("hT_ps"), sem("hT_ready")
        vec_ps, vec_ready = sem("vec_ps"), sem("vec_ready")
        qkv_ps, q_copied, kv_copied = sem("qkv_ps"), sem("q_copied"), sem("kv_copied")
        qk_ssq, qk_rstd, qk_normed = sem("qk_ssq"), sem("qk_rstd"), sem("qk_normed")
        qkT_ps, qkT_ready = sem("qkT_ps"), sem("qkT_ready")
        pool_ps, upool_ready, pooled_ready = sem("pool_ps"), sem("upool_ready"), sem("pooled_ready")
        mhalf_ready = sem("mhalf_ready")
        gate_ps, gate_copied, gates_ready = sem("gate_ps"), sem("gate_copied"), sem("gates_ready")
        score_ps, score_read, negmax_ready = sem("score_ps"), sem("score_read"), sem("negmax_ready")
        exp_done, prob_ready = sem("exp_done"), sem("prob_ready")
        probT_ps, probT_ready = sem("probT_ps"), sem("probT_ready")
        attn_ps, attn_ready = sem("attn_ps"), sem("attn_ready")
        mix_ps, mixed_ready = sem("mix_ps"), sem("mixed_ready")
        branch_ps, merged_ready = sem("branch_ps"), sem("merged_ready")
        x1_ps, x1_ready = sem("x1_ps"), sem("x1_ready")
        gffn_loaded, rw_loaded, p_loaded, gpost_loaded, rbias_loaded = (
            sem("gffn_loaded"), sem("rw_loaded"), sem("p_loaded"), sem("gpost_loaded"), sem("rbias_loaded"))
        ssq2_done, rstd2_ready, h2_ready, h2_stored = (
            sem("ssq2_done"), sem("rstd2_ready"), sem("h2_ready"), sem("h2_stored"))
        h2T_ps, h2T_ready = sem("h2T_ps"), sem("h2T_ready")
        pT_ps, pT_ready = sem("pT_ps"), sem("pT_ready")
        ple_ps, ple_copied, ple_rstd, ple_ready = (
            sem("ple_ps"), sem("ple_copied"), sem("ple_rstd"), sem("ple_ready"))
        logit_ps, logit_copied, logitT_ps, scores_ready = (
            sem("logit_ps"), sem("logit_copied"), sem("logitT_ps"), sem("scores_ready"))
        sel_ready, rank_ps, place_ready, place_used = (
            sem("sel_ready"), sem("rank_ps"), sem("place_ready"), sem("place_used"))
        tokcol_ready, list_ready, maxcnt_ready = sem("tokcol_ready"), sem("list_ready"), sem("maxcnt_ready")
        shared_ps, shared_silu, shared_act = sem("shared_ps"), sem("shared_silu"), sem("shared_act")
        shdown_ps, base_ready, base_stored = (
            sem("shdown_ps"), sem("base_ready"), [sem(f"base_stored{i}") for i in range(NT)])
        dump_stored = sem("dump_stored")
        dve_step, pool_step, act_step = sem("dve_step"), sem("pool_step"), sem("act_step")
        staged = sem("staged")
        ticket_done = [sem(f"ticket_done{n}") for n in range(2)]
        gathered = [sem(f"gathered{j}") for j in range(UNROLL)]
        hgT_ps, hgT_lo_ready, hgT_hi_ready = sem("hgT_ps"), sem("hgT_lo_ready"), sem("hgT_hi_ready")
        gu_ps, silu_ready, eact_ready = sem("gu_ps"), sem("silu_ready"), sem("eact_ready")
        eactT_ps, eactT_ready = sem("eactT_ps"), sem("eactT_ready")
        y_ps, y_ready, added = sem("y_ps"), sem("y_ready"), sem("added")
        o_loaded = [sem(f"o_loaded{n}") for n in range(3)]
        (o_iota_ready, o_place_ready, o_list_ps, o_list_ready, o_gathered, o_hgT_ps, o_hgT_lo, o_hgT_hi, o_gu_ps,
         o_silu, o_act, o_actT_ps, o_actT, o_y_ps, o_y, o_added, o_over, o_step) = (sem(f"o_{n}") for n in (
             "iota_ready", "place_ready", "list_ps", "list_ready", "gathered", "hgT_ps", "hgT_lo", "hgT_hi",
             "gu_ps", "silu", "act", "actT_ps", "actT", "y_ps", "y", "added", "over", "step"))
        experts_done = sem("experts_done")
        x2_loaded = [sem(f"x2_loaded{i}") for i in range(NT)]
        ssq3_done, rstd3_ready, rows3_ready = sem("ssq3_done"), sem("rstd3_ready"), sem("rows3_ready")
        h3T_ps, h3T_ready = sem("h3T_ps"), sem("h3T_ready")
        final_ps, sgate_ready, out_ready, out_stored = (
            sem("final_ps"), sem("sgate_ready"), sem("out_ready"), sem("out_stored"))

        def unit_source(name):
            w_in = t["w_in"][0].rearrange("(p k) n -> p k n", k=KD)
            c0 = {"q0": 512, "q1": 768, "kv": 1024, "pool0": 0, "pool1": 256}
            if name in c0:
                return w_in[:, :, c0[name]:c0[name] + 256]
            n = int(name[-1]) if name[-1].isdigit() else 0
            if name.startswith("gate"):
                return t["w_gate"][0].rearrange("(p k) n -> p k n", k=KD)[:, :, n * 256:(n + 1) * 256]
            if name[:2] in ("wa", "wb"):
                w = t["w_branch_a" if name[1] == "a" else "w_branch_b"][0]
                return w.rearrange("(k p) n -> p k n", p=P)[:, :, n * 512:(n + 1) * 512]
            if name.startswith("out"):
                return t["w_out"][0].rearrange("(k p) n -> p k n", p=P)[:, :, n * 256:(n + 1) * 256]
            if name == "shg":
                return t["w_sh_gate"][0].rearrange("(p k) n -> p k n", k=KD)
            if name == "shu":
                return t["w_sh_up"][0].rearrange("(p k) n -> p k n", k=KD)
            if name == "shd":
                return t["w_sh_down"][0].rearrange("(j p) n -> p j n", p=P)
            return t["w_ple_proj"][0].rearrange("(j p) n -> p j n", p=P)

        def unit_view(slot, k):
            return ring[:, slot, :].rearrange("p (k n) -> p k n", k=k)

        def pair_view(slot):
            return ring[:, slot:slot + 2, :].rearrange("p u (k n) -> p k u n", k=KD)

        exp_gate = t["w_exp_gate"][0].rearrange("e (p k) f -> e p (k f)", k=KD)
        exp_up = t["w_exp_up"][0].rearrange("e (p k) f -> e p (k f)", k=KD)
        exp_down = t["w_exp_down"][0].rearrange("e (p j) n -> e p (j n)", j=2)
        ple_gate = t["w_ple_gate"][0].rearrange("(p k) n -> p k n", k=KD)
        out_rows = out[0].rearrange("(i p) n -> i p n", p=P)
        x_rows = t["x"][0].rearrange("(i p) n -> i p n", p=P)
        acc_rows = acc[0:T, :].rearrange("(i p) n -> i p n", p=P)
        h2_rows = h2_dram.rearrange("(i p) n -> i p n", p=P)

        def further_rounds(eng, start, step):
            eng.wait_ge(maxcnt_ready, 1)
            longest = eng.value_load(maxcnt[0:1, 0:1], min_val=0, max_val=T)
            with eng.Fori(1, ROUNDS) as j:
                with eng.If(longest > j * CAP):
                    start(j)
                    with eng.Fori(0, NE) as e:
                        step(e, (j - 1) * NE + e, j)

        block = ctx.enter_context(nc.Block())

        @block.sync
        def _(sp):
            released_by = {"q0": (qkv_ps, 2 * NT), "q1": (qkv_ps, 2 * NT), "kv": (qkv_ps, 2 * NT),
                           "pool0": (pool_ps, 2), "pool1": (pool_ps, NG)}
            released_by |= {f"gate{c}": (gate_ps, 2 * c + 2) for c in range(8)}
            released_by |= {f"w{ab}{c}": (branch_ps, 4 * c + 4) for ab in "ab" for c in range(2)}

            def load_dense(u):
                slot = DENSE_SLOT[u]
                before = [n for n in range(u) if DENSE_SLOT[n] == slot]
                if before:
                    sp.wait_ge(*released_by[DENSE[before[-1]]])
                if slot == 8:
                    sp.wait_ge(score_read, 4 * NT)
                dst = ring[:, slot, :]
                src = unit_source(DENSE[u])
                sp.dma_start(dst.rearrange("p (k n) -> p k n", k=src.shape[1]), src
                             ).then_inc(slot_loaded[slot], 16)

            for i in range(NT):
                sp.dma_start(xrow[:, i, :], x_rows[i]).then_inc(x_loaded[i], 16)
            sp.dma_start(cst[:, :], t["constants"]).then_inc(cst_loaded, 16)
            for u in range(3):
                load_dense(u)
            sp.dma_start(bias_t.rearrange("p h k -> p (h k)"), t["alibi"]).then_inc(bias_loaded, 16)
            for u in range(3, N_DENSE - 1):
                load_dense(u)
                if u == DENSE_AT["out3"]:
                    load_dense(N_DENSE - 1)
            sp.wait_ge(merged_ready, KD)
            sp.dma_start(gffn, t["g_ffn"].broadcast_to([P, D])).then_inc(gffn_loaded, 16)
            sp.dma_start(prow, t["p"][0, 0].rearrange("(i p) n -> p i n", p=P)).then_inc(p_loaded, 16)
            sp.dma_start(rw, t["w_router"][0].rearrange("(p k) e -> p k e", k=KD)).then_inc(rw_loaded, 16)
            sp.dma_start(rbias, t["router_bias"].broadcast_to([P, NE])).then_inc(rbias_loaded, 16)

            def load_expert(e, j, turn):
                s = EXPERT_SLOT[j]
                for n, w in enumerate((exp_gate, exp_up, exp_down)):
                    if turn is not None and n == 0:
                        sp.wait_ge(gu_ps, (turn - 1) * UNROLL + j + 1)
                    if turn is not None and n == 2:
                        sp.wait_ge(y_ps, (turn - 1) * UNROLL + j + 1)
                    sp.dma_start(ring[:, s + n, :], w[bass.ds(e, 1)].rearrange("e p n -> (e p) n")
                                 ).then_inc(slot_loaded[s + n], 16)

            sp.wait_ge(probT_ps, 4 * NT)
            sp.wait_ge(attn_ps, NT)
            sp.wait_ge(mix_ps, NG)
            load_expert(0, 0, None)
            sp.wait_ge(x1_ready, 2 * NT)
            sp.dma_start(gpost, t["g_ple_post"].broadcast_to([P, D])).then_inc(gpost_loaded, 16)
            load_expert(1, 1, None)
            sp.wait_ge(shared_ps, 2)
            load_expert(2, 2, None)
            sp.wait_ge(ple_ps, NT)
            sp.wait_ge(shdown_ps, 2 * NT)
            for b in base_stored:
                sp.wait_ge(b, 16)
            for g in gathered[:AHEAD]:
                sp.wait_ge(g, 16)
            load_expert(3, 3, None)
            with sp.Fori(1, TURNS) as turn:
                for j in range(UNROLL):
                    load_expert(turn * UNROLL + j, j, turn)

            def o_start(j):
                sp.wait_ge(y_ps, NE)

            def o_load(e, n, j):
                sp.wait_ge(o_over, n + 1)
                for c, w in enumerate((exp_gate, exp_up, exp_down)):
                    sp.dma_start(ring[:, O_SLOT + c, :], w[bass.ds(e, 1)].rearrange("e p n -> (e p) n")
                                 ).then_inc(o_loaded[c], 16)

            further_rounds(sp, o_start, o_load)
            sp.wait_ge(y_ps, NE - UNROLL + 1)
            sp.wait_ge(gu_ps, NE - UNROLL + 2)
            for c, s in enumerate(TAIL_SLOT):
                sp.dma_start(unit_view(s, KD), ple_gate[:, :, c * 256:(c + 1) * 256]
                             ).then_inc(slot_loaded[s], 16)
            for i in range(NT):
                for half in range(2):
                    n = slice(half * 512, (half + 1) * 512)
                    sp.wait_ge(out_ready, 2 * i + half + 1)
                    sp.dma_start(out_rows[i][:, n], xrow[:, i, n]).then_inc(out_stored, 16)
            sp.wait_ge(out_stored, 16 * 2 * NT)

        @block.gpsimd
        def _(pool):
            n_step = [0]

            def link(ins):
                n_step[0] += 1
                ins.then_inc(pool_step, 1)
                pool.wait_ge(pool_step, n_step[0])

            def small_load(dst, src):
                pool.dma_start(dst, src).then_inc(small_loaded, 16)

            pool.dma_start(gcol[:, 0, :], t["g_mix"].rearrange("o (p k) -> (o p) k", k=KD)).then_inc(gmix_loaded, 16)
            nc.gpsimd.memset(tickets[:, 2:3], 0.0).then_inc(o_over, 1)
            nc.gpsimd.memset(mhalf[:, :], -0.5).then_inc(mhalf_ready, 1)
            nc.gpsimd.memset(upool[:, :, 0:PAD], 0.0).then_inc(mhalf_ready, 1)
            nc.gpsimd.memset(win[0][:, 0:PAD], 0.0).then_inc(mhalf_ready, 1)
            nc.gpsimd.memset(win[1][:, 0:PAD], 0.0).then_inc(mhalf_ready, 1)
            pool.wait_ge(mhalf_ready, 4)

            def rstd(ssq, width, n, done):
                link(nc.gpsimd.tensor_scalar(ssq, ssq, 1.0 / width, EPS, ALU.mult, ALU.add))
                nc.gpsimd.tensor_tensor(ssq, ssq, mhalf[:, 0:n], ALU.pow).then_inc(done, 1)

            for i in range(NT):
                pool.wait_ge(ssq_done, i + 1)
                rstd(st[:, 0, i:i + 1], D, 1, rstd_ready)
            small_load(vecs[0:16, :], t["b_gate"].rearrange("o (r n) -> (o r) n", n=P))
            small_load(vecs[16:20, :], t["pool_scale"].rearrange("o (r n) -> (o r) n", n=P))
            for n, v in ((20, "q_gain"), (21, "k_gain")):
                for c in range(2):
                    small_load(vecs[n:n + 1, c * DH:(c + 1) * DH], t[v])
            small_load(gcol[:, 1, :], t["g_ple"].rearrange("o (p k) -> (o p) k", k=KD))
            small_load(sink_in[:, :], t["attn_sinks"].broadcast_to([P, NH]))
            small_load(mixw[:, :, :], t["w_pool_mix"][0].rearrange("g c d -> c g d"))
            for i in range(NT):
                pool.wait_ge(qk_ssq, i + 1)
                rstd(st[:, 3, 0:NH + NKV], DH, NH + NKV, qk_rstd)

            for g, w in enumerate(POOL_WINDOWS):
                pool.wait_ge(upool_ready, g + 1)
                src, span, k = upool[:, g, :], 1, 0
                while span < w:
                    link(nc.gpsimd.tensor_tensor(win[k][:, PAD:], src[:, PAD:], src[:, PAD - span:PAD + T - span],
                                                 ALU.add))
                    src, span, k = win[k], 2 * span, 1 - k
                link(nc.gpsimd.tensor_tensor(win[k][:, PAD:2 * PAD], src[:, PAD:2 * PAD],
                                             cst[:, C_IC + g * PAD:C_IC + (g + 1) * PAD], ALU.mult))
                link(nc.gpsimd.tensor_scalar(win[k][:, 2 * PAD:], src[:, 2 * PAD:], 1.0 / w, None, ALU.mult))
                ins = nc.gpsimd.tensor_tensor(pooled[:, g, :], win[k][:, PAD:], upool[:, g, PAD:], ALU.subtract)
                ins.then_inc(pooled_ready, 1)
                pool.wait_ge(pooled_ready, g + 1)

            for i in range(NT):
                pool.wait_ge(ssq2_done, i + 1)
                rstd(st[:, 1, i:i + 1], D, 1, rstd2_ready)
            for i in range(NT):
                pool.wait_ge(ple_copied, i + 1)
                rstd(st[:, 2, i:i + 1], D, 1, ple_rstd)

            def ticket(n, done):
                nc.gpsimd.tensor_tensor(tickets[:, n:n + 1], cst[:, C_P:C_P + 1], cst[:, C_P:C_P + 1], ALU.add
                                        ).then_inc(done, 1)

            def stage_index(kind, e, j):
                nc.gpsimd.tensor_copy(stage[:, kind, j, :], slot_ix[:, bass.ds(e, 1)]).then_inc(staged, 1)

            def gather(e, j):
                pool.indirect_dma_start(hg[j][0:CAP, :], None, h2_dram,
                                        bass.IndirectOffsetOnAxis(ap=stage[0:CAP, 0, j, :], axis=0),
                                        bounds_check=T - 1, oob_is_err=False).then_inc(gathered[j], 16)

            def scatter(e, j, first=False):
                if not first:
                    pool.wait_ge(ticket_done[1], e)
                    pool.wait_ge(added, 16 * e)
                pool.wait_ge(y_ready, e + 1)
                ticket(1, ticket_done[1])
                pool.indirect_dma_start(acc, bass.IndirectOffsetOnAxis(ap=stage[0:CAP, 1, j, :], axis=0),
                                        yrow[j][0:CAP, :], None, compute_op=ALU.add).then_inc(added, 16)

            def move(e, j, first=False):
                if not first:
                    pool.wait_ge(hgT_ps, 2 * e)
                stage_index(0, e + AHEAD, (j + AHEAD) % UNROLL)
                stage_index(1, e + 1, (j + 1) % UNROLL)
                if not first:
                    pool.wait_ge(ticket_done[0], e)
                pool.wait_ge(staged, 2 * e + AHEAD + 3)
                ticket(0, ticket_done[0])
                gather(e + AHEAD, (j + AHEAD) % UNROLL)
                scatter(e, j, first)

            pool.wait_ge(list_ready, 1)
            pool.wait_ge(h2_stored, 16 * NT)
            for e in range(AHEAD):
                stage_index(0, e, e)
            stage_index(1, 0, 0)
            pool.wait_ge(staged, AHEAD + 1)
            for e in range(AHEAD):
                pool.wait_ge(base_stored[e], 16)
                gather(e, e)
            for b in base_stored:
                pool.wait_ge(b, 16)
            pool.wait_ge(dump_stored, 16)
            for e in range(UNROLL):
                move(e, e, first=(e == 0))
            with pool.Fori(1, TURNS - 1) as turn:
                for j in range(UNROLL):
                    move(turn * UNROLL + j, j)
            n_staged = 2 * (NE - UNROLL) + AHEAD + 1
            for e in range(NE - UNROLL, NE):
                if e + AHEAD < NE:
                    move(e, e % UNROLL)
                    n_staged += 2
                else:
                    if e + 1 < NE:
                        stage_index(1, e + 1, (e + 1) % UNROLL)
                        n_staged += 1
                        pool.wait_ge(staged, n_staged)
                    scatter(e, e % UNROLL)

            def o_start(j):
                pool.wait_ge(added, 16 * NE)

            def o_move(e, n, j):
                pool.wait_ge(o_over, n + 1)
                pool.wait_ge(ticket_done[0], NE - AHEAD + n)
                pool.wait_ge(o_list_ready, n + 1)
                ticket(0, ticket_done[0])
                pool.indirect_dma_start(hg[0][0:CAP, :], None, h2_dram,
                                        bass.IndirectOffsetOnAxis(ap=o_ix[0:CAP, :], axis=0),
                                        bounds_check=T - 1, oob_is_err=False).then_inc(o_gathered, 16)
                pool.wait_ge(ticket_done[1], NE + n)
                pool.wait_ge(o_y, n + 1)
                ticket(1, ticket_done[1])
                pool.indirect_dma_start(acc, bass.IndirectOffsetOnAxis(ap=o_ix[0:CAP, :], axis=0),
                                        yrow[0][0:CAP, :], None, compute_op=ALU.add).then_inc(o_added, 16)
                pool.wait_ge(o_added, 16 * (n + 1))
                ticket(2, o_over)

            further_rounds(pool, o_start, o_move)
            pool.wait_ge(added, 16 * NE)
            nc.gpsimd.memset(tickets[:, 3:4], 0.0).then_inc(experts_done, 1)
            for i in range(NT):
                pool.wait_ge(ssq3_done, i + 1)
                rstd(st[:, 0, 8 + i:9 + i], D, 1, rstd3_ready)

        @block.scalar
        def _(act):
            for i in range(NT):
                act.wait_ge(x_loaded[i], 16)
                nc.scalar.activation(rows[:, i, :], xrow[:, i, :], ACT.Square,
                                     accum_out=st[:, 0, i:i + 1]).then_inc(ssq_done, 1)
            act.dma_start(acc[DUMP:DUMP + P, :], xrow[:, 0, :]).then_inc(dump_stored, 16)
            for i in range(NT):
                act.wait_ge(qkv_ps, 2 * i + 1)
                nc.scalar.activation(rows[:, i, 0:QD], bank(2 * (i % 2)), ACT.Copy).then_inc(q_copied, 1)
            act.wait_ge(mhalf_ready, 4)
            for g in range(NG):
                act.wait_ge(pool_ps, g + 1)
                nc.scalar.activation(upool[:, g, PAD:], bank(g), ACT.Copy).then_inc(upool_ready, 1)

            def exps(n):
                act.wait_ge(negmax_ready, n + 1)
                o = P if n == 0 else 0
                for h in range(NH):
                    nc.scalar.activation(score[:, h, o:], score[:, h, o:], ACT.Exp, bias=smx[:, 1, h:h + 1],
                                         accum_out=smx[:, 2, h:h + 1])
                nc.scalar.activation(smx[:, 4, :], smx[:, 3, :], ACT.Exp).then_inc(exp_done, 1)

            def gate_copy(m):
                act.wait_ge(gate_ps, m + 1)
                if m == 0:
                    act.wait_ge(vec_ready, 1)
                nc.scalar.activation(gates[:, m, :], bank(m % 2), ACT.Identity,
                                     bias=vecT[:, m:m + 1]).then_inc(gate_copied, 1)

            exps(0)
            for m in range(2 * KD):
                gate_copy(m)
                if m in (1, 3, 5):
                    exps((m + 1) // 2)
                if m == 13:
                    for g in range(NG):
                        act.wait_ge(mix_ps, g + 1)
                        nc.scalar.activation(mixedT[:, g, :], bank(2 + g), ACT.Copy,
                                             scale=vecT[:, 16 + g:17 + g]).then_inc(mixed_ready, 1)
            act.wait_ge(gate_copied, 2 * KD)
            for m in range(KD):
                for half in range(2):
                    c = m + half * KD
                    nc.scalar.activation(gates[:, c, :], gates[:, c, :], ACT.Sigmoid).then_inc(gates_ready, 1)

            for i in range(NT):
                act.wait_ge(x1_ready, 2 * i + 2)
                nc.scalar.activation(rows[:, i, :], xrow[:, i, :], ACT.Square,
                                     accum_out=st[:, 1, i:i + 1]).then_inc(ssq2_done, 1)
                if i:
                    act.wait_ge(h2_ready, i)
                    act.dma_start(h2_rows[i - 1], rows[:, i - 1, :]).then_inc(h2_stored, 16)

            act.wait_ge(h2_ready, NT)
            act.dma_start(h2_rows[NT - 1], rows[:, NT - 1, :]).then_inc(h2_stored, 16)

            def ple_copy(i):
                act.wait_ge(ple_ps, i + 1)
                b = 2 if i % 2 == 0 else 4
                nc.scalar.activation(pp[:, i, :], bank(b, 2), ACT.Square,
                                     accum_out=st[:, 2, i:i + 1]).then_inc(act_step, 1)
                act.wait_ge(act_step, i + 1)
                nc.scalar.activation(pp[:, i, :], bank(b, 2), ACT.Copy).then_inc(ple_copied, 1)

            ple_copy(0)
            act.wait_ge(logit_ps, 1)
            act.wait_ge(x1_ready, 2 * NT)
            nc.scalar.activation(r_lt, ps[0:NE, 0:T], ACT.Copy).then_inc(logit_copied, 1)
            act.wait_ge(logitT_ps, 1)
            nc.scalar.activation(r_sc, ps[:, 512:512 + NR], ACT.Sigmoid).then_inc(scores_ready, 1)
            for i in range(1, NT):
                ple_copy(i)
            for f in range(2):
                act.wait_ge(shared_ps, f + 1)
                nc.scalar.activation(sh_silu[:, f, :], bank(2 + 2 * f), ACT.Silu).then_inc(shared_silu, 1)

            for i in range(NT):
                act.wait_ge(base_ready, 2 * i + 2)
                act.dma_start(acc_rows[i], xrow[:, i, :]).then_inc(base_stored[i], 16)

            def rows_hi(e, j):
                k = j % 2
                act.wait_ge(hgT_ps, 2 * e + 2)
                nc.scalar.activation(hgT[k][:, 4:8, :], bank(1)[:, 0:4 * CAP].rearrange("p (k n) -> p k n", k=4),
                                     ACT.Copy).then_inc(hgT_hi_ready, 1)

            def silu(e, k):
                act.wait_ge(gu_ps, e + 1)
                nc.scalar.activation(esilu[k][0:CAP, :], bank(2 + k)[0:CAP, 0:FE], ACT.Silu
                                     ).then_inc(silu_ready, 1)

            def weigh(e, j):
                act.wait_ge(y_ps, e + 1)
                nc.scalar.activation(yrow[j][0:CAP, :], bank(6, 2)[0:CAP, :], ACT.Copy,
                                     scale=slot_w[0:CAP, bass.ds(e, 1)]).then_inc(y_ready, 1)

            act.wait_ge(list_ready, 1)
            act.wait_ge(h2_stored, 16 * NT)
            act.wait_ge(shdown_ps, 2 * NT)
            rows_hi(0, 0)
            silu(0, 0)
            rows_hi(1, 1)
            silu(1, 1)
            rows_hi(2, 2)
            weigh(0, 0)
            for e in range(2, UNROLL):
                silu(e, e % 2)
                rows_hi(e + 1, e + 1)
                weigh(e - 1, e - 1)
            with act.Fori(1, TURNS - 1) as turn:
                for j in range(UNROLL):
                    e = turn * UNROLL + j
                    silu(e, j % 2)
                    rows_hi(e + 1, j + 1)
                    act.wait_ge(added, 16 * (e - 3))
                    weigh(e - 1, (j - 1) % UNROLL)
            for e in range(NE - UNROLL, NE):
                silu(e, e % 2)
                if e + 1 < NE:
                    rows_hi(e + 1, e + 1)
                act.wait_ge(added, 16 * (e - 3))
                weigh(e - 1, (e - 1) % UNROLL)
            act.wait_ge(added, 16 * (NE - 3))
            weigh(NE - 1, (NE - 1) % UNROLL)

            def o_start(j):
                act.wait_ge(added, 16 * NE)

            def o_scalar(e, n, j):
                act.wait_ge(o_over, n + 1)
                act.wait_ge(o_hgT_ps, 2 * n + 2)
                nc.scalar.activation(hgT[0][:, 4:8, :], bank(1)[:, 0:4 * CAP].rearrange("p (k n) -> p k n", k=4),
                                     ACT.Copy).then_inc(o_hgT_hi, 1)
                act.wait_ge(o_gu_ps, n + 1)
                nc.scalar.activation(esilu[0][0:CAP, :], bank(2)[0:CAP, 0:FE], ACT.Silu).then_inc(o_silu, 1)
                act.wait_ge(o_y_ps, n + 1)
                nc.scalar.activation(yrow[0][0:CAP, :], bank(6, 2)[0:CAP, :], ACT.Copy,
                                     scale=o_lst[0:CAP, LCOL + 1:LCOL + 2]).then_inc(o_y, 1)

            further_rounds(act, o_start, o_scalar)

            act.wait_ge(experts_done, 1)
            for i in range(NT):
                act.dma_start(xrow[:, i, :], acc_rows[i]).then_inc(x2_loaded[i], 16)
            for i in range(NT):
                act.wait_ge(x2_loaded[i], 16)
                nc.scalar.activation(rows[:, i, :], xrow[:, i, :], ACT.Square,
                                     accum_out=st[:, 0, 8 + i:9 + i]).then_inc(ssq3_done, 1)
            for i in range(NT):
                for half in range(2):
                    act.wait_ge(final_ps, 2 * i + half + 1)
                    if i >= 2:
                        act.wait_ge(out_ready, 2 * i - 3 + half)
                    nc.scalar.activation(sgate[i % 2][:, half * 512:(half + 1) * 512], bank(half), ACT.Sigmoid
                                         ).then_inc(sgate_ready, 1)

        @block.vector
        def _(dve):
            n_step = [0]

            def link(ins):
                n_step[0] += 1
                ins.then_inc(dve_step, 1)
                dve.wait_ge(dve_step, n_step[0])

            def first_rows(i):
                dve.wait_ge(rstd_ready, i + 1)
                nc.vector.tensor_scalar(rows[:, i, :], xrow[:, i, :], st[:, 0, i:i + 1], None, ALU.mult
                                        ).then_inc(rows_ready, 1)

            def first_T(i):
                for half in range(2):
                    dve.wait_ge(hT_ps, 2 * i + half + 1)
                    if i == 0 and half == 0:
                        dve.wait_ge(gmix_loaded, 16)
                    nc.vector.tensor_tensor(
                        actT[:, 4 * half:4 * half + 4, i * P:(i + 1) * P],
                        bank(2 * i + half).rearrange("p (k n) -> p k n", k=4),
                        gcol[:, 0, 4 * half:4 * half + 4].unsqueeze(2).broadcast_to([P, 4, P]), ALU.mult
                    ).then_inc(hT_ready, 1)

            for i in range(NT):
                first_rows(i)
                if i:
                    first_T(i - 1)
            first_T(NT - 1)

            nc.vector.tensor_copy(triT[:, :], cst[:, C_SLT:C_SLT + P])
            nc.vector.tensor_copy(oneT[:, :], cst[:, C_ONE:C_ONE + P])

            def qk_transposed(i):
                dve.wait_ge(qkT_ps, i + 1)
                if i == 0:
                    dve.wait_ge(vec_ready, 1)
                b = 4 + 2 * (i % 2)
                cols = slice(i * P, (i + 1) * P)
                nc.vector.tensor_scalar(qT[:, :, cols], bank(b).rearrange("p (a n) -> p a n", a=4),
                                        vecT[:, 20:21], None, ALU.mult)
                nc.vector.tensor_scalar(kT[:, :, cols], bank(b + 1)[:, 0:2 * P].rearrange("p (a n) -> p a n", a=2),
                                        vecT[:, 21:22], None, ALU.mult).then_inc(qkT_ready, 1)

            NQK = NH + NKV
            for i in range(NT):
                dve.wait_ge(qkv_ps, 2 * i + 2)
                nc.vector.tensor_copy(rows[:, i, QD:QD + 2 * KVD], bank(2 * (i % 2) + 1)[:, 0:2 * KVD]
                                      ).then_inc(kv_copied, 1)
                dve.wait_ge(kv_copied, i + 1)
                dve.wait_ge(q_copied, i + 1)
                qk = rows[:, i, 0:QD + KVD]
                link(nc.vector.tensor_tensor(qsq, qk, qk, ALU.mult))
                nc.vector.tensor_reduce(st[:, 3, 0:NQK], qsq.rearrange("p (h d) -> p h d", h=NQK), AX_X, ALU.add
                                        ).then_inc(qk_ssq, 1)
                dve.wait_ge(qk_rstd, i + 1)
                qk3 = qk.rearrange("p (h d) -> p h d", h=NQK)
                for kv in range(NKV):
                    nc.vector.tensor_scalar(
                        rows[:, i, 768 + kv * P:768 + (kv + 1) * P].rearrange("p (c d) -> p c d", c=2),
                        qk3[:, NH + kv, :].unsqueeze(1).broadcast_to([P, 2, DH]),
                        st[:, 3, NH + kv:NH + kv + 1], None, ALU.mult)
                nc.vector.tensor_tensor(qk3[:, 0:NH, :], qk3[:, 0:NH, :],
                                        st[:, 3, 0:NH].unsqueeze(2).broadcast_to([P, NH, DH]), ALU.mult
                                        ).then_inc(qk_normed, 1)
                if i < NT - 1:
                    dve.wait_ge(qk_normed, i + 1)
                if i == 1:
                    dve.wait_ge(vec_ps, 1)
                    nc.vector.tensor_copy(vecT[:, :], bank(7)[:, 0:NVEC]).then_inc(vec_ready, 1)
                    nc.vector.tensor_copy(sink[:, :].rearrange("p (kv par half) -> p kv par half", kv=2, par=2),
                                          sink_in[:, :].rearrange("p (kv half par) -> p kv par half", kv=2, half=2)
                                          ).then_inc(dve_step, 1)
                    n_step[0] += 1
                if i:
                    qk_transposed(i - 1)
            qk_transposed(NT - 1)

            def softmax_scores(n):
                o = P if n == 0 else 0
                if n == 0:
                    dve.wait_ge(bias_loaded, 16)
                else:
                    dve.wait_ge(probT_ps, 4 * n)
                for b in range(4):
                    dve.wait_ge(score_ps, 4 * n + b + 1)
                    nc.vector.scalar_tensor_tensor(
                        score[:, 2 * b:2 * b + 2, o:],
                        bank(2 + b).rearrange("p (h k) -> p h k", h=2)[:, :, o:], DH ** -0.5,
                        bias_t[:, 2 * b:2 * b + 2, o:], ALU.mult, ALU.add).then_inc(score_read, 1)
                dve.wait_ge(score_read, 4 * n + 4)
                link(nc.vector.tensor_reduce(smx[:, 0, :], score[:, :, o:], AX_X, ALU.max))
                link(nc.vector.tensor_tensor(smx[:, 0, :], smx[:, 0, :], sink[:, :], ALU.max))
                nc.vector.tensor_tensor(smx[:, 3, :], sink[:, :], smx[:, 0, :], ALU.subtract)
                nc.vector.tensor_scalar(smx[:, 1, :], smx[:, 0, :], -1.0, None, ALU.mult).then_inc(negmax_ready, 1)

            def softmax_divide(n):
                o = P if n == 0 else 0
                dve.wait_ge(exp_done, n + 1)
                link(nc.vector.tensor_tensor(smx[:, 5, :], smx[:, 2, :], smx[:, 4, :], ALU.add))
                link(nc.vector.reciprocal(smx[:, 6, :], smx[:, 5, :]))
                nc.vector.tensor_tensor(score[:, :, o:], score[:, :, o:],
                                        smx[:, 6, :].unsqueeze(2).broadcast_to([P, NH, 2 * P - o]), ALU.mult
                                        ).then_inc(prob_ready, 1)

            def prob_transposed(n):
                o = 2 * P if n == 0 else 0
                if n:
                    dve.wait_ge(attn_ps, n)
                for b in range(4):
                    dve.wait_ge(probT_ps, 4 * n + b + 1)
                    nc.vector.tensor_copy(probT[:, b, o:], bank(6 + b % 2)[:, o:]).then_inc(probT_ready, 1)

            def attn_copy(n):
                dve.wait_ge(attn_ps, n + 1)
                nc.vector.tensor_copy(qT[:, :, n * P:(n + 1) * P], bank(6).rearrange("p (a n) -> p a n", a=4)
                                      ).then_inc(attn_ready, 1)

            softmax_scores(0)
            for n in range(NT):
                softmax_divide(n)
                prob_transposed(n)
                if n + 1 < NT:
                    softmax_scores(n + 1)
                attn_copy(n)

            for m in range(KD):
                b = 2 + 2 * (m % 2)
                dve.wait_ge(branch_ps, m + 1)
                dve.wait_ge(gates_ready, 2 * m + 2)
                nc.vector.tensor_tensor(gates[:, m, :], gates[:, m, :], bank(b), ALU.mult).then_inc(dve_step, 1)
                nc.vector.tensor_tensor(gates[:, KD + m, :], gates[:, KD + m, :], bank(b + 1), ALU.mult
                                        ).then_inc(dve_step, 1)
                n_step[0] += 2
                dve.wait_ge(dve_step, n_step[0])
                nc.vector.tensor_tensor(gates[:, m, :], gates[:, m, :], gates[:, KD + m, :], ALU.add
                                        ).then_inc(merged_ready, 1)

            dve.wait_ge(dump_stored, 16)

            def residual(i):
                for half in range(2):
                    dve.wait_ge(x1_ps, 2 * i + half + 1)
                    xs = xrow[:, i, half * 512:(half + 1) * 512]
                    nc.vector.tensor_tensor(xs, xs, bank(half), ALU.add).then_inc(x1_ready, 1)

            def second_rows(i):
                if i == 0:
                    dve.wait_ge(gffn_loaded, 16)
                dve.wait_ge(rstd2_ready, i + 1)
                dve.wait_ge(x1_ready, 2 * i + 2)
                nc.vector.scalar_tensor_tensor(rows[:, i, :], xrow[:, i, :], st[:, 1, i:i + 1], gffn,
                                               ALU.mult, ALU.mult).then_inc(h2_ready, 1)

            def second_T(i):
                for half in range(2):
                    dve.wait_ge(h2T_ps, 2 * i + half + 1)
                    nc.vector.tensor_copy(actT[:, 4 * half:4 * half + 4, i * P:(i + 1) * P],
                                          bank(2 + 2 * (i % 2) + half).rearrange("p (k n) -> p k n", k=4)
                                          ).then_inc(h2T_ready, 1)

            residual(0)
            residual(1)
            second_rows(0)
            residual(2)
            second_T(0)
            second_rows(1)
            residual(3)
            second_T(1)
            second_rows(2)
            second_rows(3)
            second_T(2)
            for j in range(2):
                dve.wait_ge(pT_ps, j + 1)
                nc.vector.tensor_copy(pT[:, j, :], bank(6 + j)).then_inc(pT_ready, 1)
            second_T(3)

            def ple_scale(i):
                if i == 0:
                    dve.wait_ge(gpost_loaded, 16)
                dve.wait_ge(ple_rstd, i + 1)
                nc.vector.scalar_tensor_tensor(pp[:, i, :], pp[:, i, :], st[:, 2, i:i + 1], gpost,
                                               ALU.mult, ALU.mult).then_inc(ple_ready, 1)

            dve.wait_ge(scores_ready, 1)
            dve.wait_ge(rbias_loaded, 16)
            link(nc.vector.tensor_tensor(choice.rearrange("p (i e) -> p i e", i=NT),
                                         r_sc.rearrange("p (i e) -> p i e", i=NT),
                                         rbias.unsqueeze(1).broadcast_to([P, NT, NE]), ALU.add))
            g84 = repl
            G3 = NT * NEG
            for n in range(G3):
                nc.vector.max(g84[:, n * EPG:(n + 1) * EPG], choice[:, n * EPG:(n + 1) * EPG]
                              ).then_inc(dve_step, 1)
            n_step[0] += G3
            dve.wait_ge(dve_step, n_step[0])
            g3 = g84.rearrange("p (g s) -> p g s", s=EPG)
            gsum = small[:, 0:G3]
            gsort = small[:, G3:G3 + NEG]
            link(nc.vector.tensor_tensor(gsum, g3[:, :, 0], g3[:, :, 1], ALU.add))
            gm = masked[:, 0:G3]
            gix = masked[:, G3:G3 + NEG].bitcast(U32)
            gixf = masked[:, 2 * G3:2 * G3 + NEG]
            eq = masked[:, 3 * G3:4 * G3]
            for i in range(NT):
                gi = gsum[:, i * NEG:(i + 1) * NEG]
                link(nc.vector.max(gsort, gi))
                link(nc.vector.max_index(gix, gsort, gi))
                link(nc.vector.tensor_copy(gixf, gix))
                eq3 = eq.rearrange("p (g s) -> p g s", s=TOPG)
                link(nc.vector.tensor_tensor(
                    eq3, cst[:, C_IOTA8:C_IOTA8 + NEG].unsqueeze(2).broadcast_to([P, NEG, TOPG]),
                    gixf[:, 0:TOPG].unsqueeze(1).broadcast_to([P, NEG, TOPG]), ALU.is_equal))
                link(nc.vector.tensor_reduce(gm[:, i * NEG:(i + 1) * NEG], eq3, AX_X, ALU.add))
            c3 = choice.rearrange("p (g s) -> p g s", s=EPG)
            r3 = repl.rearrange("p (g s) -> p g s", s=EPG)
            link(nc.vector.tensor_tensor(r3, c3, gm.unsqueeze(2).broadcast_to([P, G3, EPG]), ALU.mult))
            link(nc.vector.tensor_scalar(gsum, gm, -1.0, BIG, ALU.add, ALU.mult))
            link(nc.vector.tensor_tensor(masked.rearrange("p (g s) -> p g s", s=EPG), r3,
                                         gsum.unsqueeze(2).broadcast_to([P, G3, EPG]), ALU.add))
            for i in range(NT):
                mi = masked[:, i * NE:(i + 1) * NE]
                link(nc.vector.max(gsort, mi))
                link(nc.vector.match_replace(repl[:, i * NE:(i + 1) * NE], gsort, mi, -BIG / 2))
            link(nc.vector.tensor_tensor(r_sel, repl, masked, ALU.not_equal))
            nc.vector.tensor_copy(selb, r_sel).then_inc(sel_ready, 1)
            link(nc.vector.tensor_tensor(r_w, r_sc, r_sel, ALU.mult))
            w3 = r_w.rearrange("p (i e) -> p i e", i=NT)
            wsum = small[:, 0:NT]
            link(nc.vector.tensor_reduce(wsum, w3, AX_X, ALU.add))
            link(nc.vector.tensor_scalar(wsum, wsum, 1e-20, None, ALU.add))
            link(nc.vector.reciprocal(wsum, wsum))
            link(nc.vector.tensor_scalar(wsum, wsum, ROUTED_SCALE, None, ALU.mult))
            link(nc.vector.tensor_tensor(w3, w3, wsum.unsqueeze(2).broadcast_to([P, NT, NE]), ALU.mult))
            tc3 = tokcol.rearrange("p i e c -> p (i e) c")
            nc.vector.memset(tokcol[:, :, :, 0], 1.0)
            nc.vector.tensor_copy(tokcol[:, :, :, 1].rearrange("p i e -> p (i e)"),
                                  cst[:, C_P:C_P + 1].broadcast_to([P, NR]))
            nc.vector.tensor_copy(tokcol[:, :, :, 2], cst[:, C_TILE:C_TILE + NT].unsqueeze(2).broadcast_to([P, NT, NE]))
            rest = choice
            link(nc.vector.tensor_copy(tc3[:, :, 3], r_w))
            link(nc.vector.tensor_tensor(rest, r_w, tc3[:, :, 3], ALU.subtract))
            link(nc.vector.tensor_copy(tc3[:, :, 4], rest))
            link(nc.vector.tensor_tensor(rest, rest, tc3[:, :, 4], ALU.subtract))
            nc.vector.tensor_copy(tc3[:, :, 5], rest).then_inc(tokcol_ready, 1)
            dve.wait_ge(rank_ps, 1)
            link(nc.vector.scalar_tensor_tensor(r_rank, bank(1)[:, 0:NR], 1.0, r_sel, ALU.add, ALU.mult))
            link(nc.vector.tensor_scalar(r_rank, r_rank, -1.0, None, ALU.add))
            link(nc.vector.tensor_reduce(small[:, 8:9], bank(1)[:, NR:NR + NE], AX_X, ALU.max))
            nc.vector.tensor_copy(maxcnt[:, :], small[:, 8:9]).then_inc(maxcnt_ready, 1)
            rank3 = r_rank.rearrange("p (i e) -> p i e", i=NT)

            def places(c):
                if c >= 2:
                    dve.wait_ge(place_used, c - 1)
                for i in range(NT):
                    nc.vector.tensor_tensor(
                        place[:, c % 2, i, :, :],
                        cst[:, C_IOTA:C_IOTA + CAP].unsqueeze(1).broadcast_to([P, CHUNK, CAP]),
                        rank3[:, i, c * CHUNK:(c + 1) * CHUNK].unsqueeze(2).broadcast_to([P, CHUNK, CAP]),
                        ALU.is_equal).then_inc(place_ready, 1)

            def shared_mult(f):
                dve.wait_ge(shared_silu, f + 1)
                nc.vector.tensor_tensor(sh_act[:, f, :], sh_silu[:, f, :], bank(3 + 2 * f), ALU.mult
                                        ).then_inc(shared_act, 1)

            def base(i):
                for half in range(2):
                    dve.wait_ge(shdown_ps, 2 * i + half + 1)
                    xs = xrow[:, i, half * 512:(half + 1) * 512]
                    nc.vector.tensor_tensor(xs, xs, bank(2 + 2 * (i % 2) + half), ALU.add
                                            ).then_inc(base_ready, 1)

            places(0)
            places(1)
            ple_scale(0)
            shared_mult(0)
            places(2)
            ple_scale(1)
            shared_mult(1)
            places(3)
            base(0)
            places(4)
            base(1)
            for c in range(5, NE // CHUNK):
                places(c)

            dve.wait_ge(place_used, NE // CHUNK)
            dve.wait_ge(h2_stored, 16 * NT)
            link(nc.vector.tensor_copy(lists_sb[0:CAP], bank(6)[0:CAP, 0:NE * LCOL].rearrange(
                "p (e c) -> p e c", c=LCOL)))
            L = lists_sb[0:CAP]
            a, b_, w_, v_ = (x[0:CAP, :] for x in ltmp)
            link(nc.vector.scalar_tensor_tensor(a, L[:, :, 2], float(P), L[:, :, 1], ALU.mult, ALU.add))
            link(nc.vector.tensor_scalar(b_, L[:, :, 0], -1.0, cst[0:CAP, C_NDUMP:C_NDUMP + 1], ALU.add, ALU.mult))
            link(nc.vector.tensor_tensor(v_, L[:, :, 3], L[:, :, 4], ALU.add))
            link(nc.vector.memset(slot_ix[:, :], DUMP))
            link(nc.vector.tensor_tensor(slot_ix[0:CAP, :], a, b_, ALU.add))
            nc.vector.tensor_tensor(slot_w[0:CAP, :], v_, L[:, :, 5], ALU.add).then_inc(list_ready, 1)
            base(2)
            base(3)

            def rows_T(e, k):
                dve.wait_ge(hgT_ps, 2 * e + 1)
                nc.vector.tensor_copy(hgT[k][:, 0:4, :], bank(0)[:, 0:4 * CAP].rearrange("p (k n) -> p k n", k=4)
                                      ).then_inc(hgT_lo_ready, 1)

            def act_rows(e, k):
                dve.wait_ge(silu_ready, e + 1)
                nc.vector.tensor_tensor(eact[k][0:CAP, :], esilu[k][0:CAP, :], bank(2 + k)[0:CAP, FE:2 * FE],
                                        ALU.mult).then_inc(eact_ready, 1)

            def act_T(e, k):
                dve.wait_ge(eactT_ps, e + 1)
                nc.vector.tensor_copy(eactT[k], bank(4)[:, 0:2 * CAP].rearrange("p (j n) -> p j n", j=2)
                                      ).then_inc(eactT_ready, 1)

            dve.wait_ge(shdown_ps, 2 * NT)
            rows_T(0, 0)
            ple_scale(2)
            ple_scale(3)
            act_rows(0, 0)
            rows_T(1, 1)
            for e in range(1, UNROLL):
                act_T(e - 1, (e - 1) % 2)
                act_rows(e, e % 2)
                rows_T(e + 1, (e + 1) % 2)
            with dve.Fori(1, TURNS - 1) as turn:
                for j in range(UNROLL):
                    e = turn * UNROLL + j
                    act_T(e - 1, (j - 1) % 2)
                    act_rows(e, j % 2)
                    rows_T(e + 1, (j + 1) % 2)
            for e in range(NE - UNROLL, NE):
                act_T(e - 1, (e - 1) % 2)
                act_rows(e, e % 2)
                if e + 1 < NE:
                    rows_T(e + 1, (e + 1) % 2)
            act_T(NE - 1, (NE - 1) % 2)

            nc.vector.tensor_copy(o_iota[:, :], cst[:, C_IOTA:C_IOTA + CAP]).then_inc(o_iota_ready, 1)

            def o_start(j):
                dve.wait_ge(added, 16 * NE)
                dve.wait_ge(o_over, (j - 1) * NE + 1)
                dve.wait_ge(o_iota_ready, j)
                nc.vector.tensor_scalar(o_iota[:, :], o_iota[:, :], float(CAP), None, ALU.add
                                        ).then_inc(o_iota_ready, 1)

            def o_vector(e, n, j):
                dve.wait_ge(o_over, n + 1)
                dve.wait_ge(o_iota_ready, j + 1)
                nc.vector.tensor_tensor(o_place, o_iota[:, :].unsqueeze(1).broadcast_to([P, NT, CAP]),
                                        rank3[:, :, bass.ds(e, 1)].broadcast_to([P, NT, CAP]), ALU.is_equal
                                        ).then_inc(o_place_ready, 1)
                steps = [0]

                def o_link(ins):
                    steps[0] += 1
                    ins.then_inc(o_step, 1)
                    dve.wait_ge(o_step, n * 5 + steps[0])

                L = o_lst[0:CAP, :]
                dve.wait_ge(o_list_ps, n + 1)
                o_link(nc.vector.tensor_copy(L[:, 0:LCOL], bank(5)[0:CAP, 0:LCOL]))
                row, weight, empty = (L[:, LCOL + c:LCOL + c + 1] for c in range(3))
                o_link(nc.vector.scalar_tensor_tensor(row, L[:, 2:3], float(P), L[:, 1:2], ALU.mult, ALU.add))
                o_link(nc.vector.tensor_tensor(weight, L[:, 3:4], L[:, 4:5], ALU.add))
                o_link(nc.vector.tensor_tensor(weight, weight, L[:, 5:6], ALU.add))
                o_link(nc.vector.tensor_scalar(empty, L[:, 0:1], -1.0, cst[0:CAP, C_NDUMP:C_NDUMP + 1],
                                               ALU.add, ALU.mult))
                nc.vector.tensor_tensor(o_ix[0:CAP, :], row, empty, ALU.add).then_inc(o_list_ready, 1)
                dve.wait_ge(o_hgT_ps, 2 * n + 1)
                nc.vector.tensor_copy(hgT[0][:, 0:4, :], bank(0)[:, 0:4 * CAP].rearrange("p (k n) -> p k n", k=4)
                                      ).then_inc(o_hgT_lo, 1)
                dve.wait_ge(o_silu, n + 1)
                nc.vector.tensor_tensor(eact[0][0:CAP, :], esilu[0][0:CAP, :], bank(2)[0:CAP, FE:2 * FE],
                                        ALU.mult).then_inc(o_act, 1)
                dve.wait_ge(o_actT_ps, n + 1)
                nc.vector.tensor_copy(eactT[0], bank(4)[:, 0:2 * CAP].rearrange("p (j n) -> p j n", j=2)
                                      ).then_inc(o_actT, 1)

            further_rounds(dve, o_start, o_vector)

            def third_rows(i):
                dve.wait_ge(rstd3_ready, i + 1)
                nc.vector.tensor_scalar(rows[:, i, :], xrow[:, i, :], st[:, 0, 8 + i:9 + i], None, ALU.mult
                                        ).then_inc(rows3_ready, 1)

            def third_T(i):
                for half in range(2):
                    dve.wait_ge(h3T_ps, 2 * i + half + 1)
                    nc.vector.tensor_tensor(
                        actT[:, 4 * half:4 * half + 4, i * P:(i + 1) * P],
                        bank(2 + 2 * (i % 2) + half).rearrange("p (k n) -> p k n", k=4),
                        gcol[:, 1, 4 * half:4 * half + 4].unsqueeze(2).broadcast_to([P, 4, P]), ALU.mult
                    ).then_inc(h3T_ready, 1)

            def result(i):
                for half in range(2):
                    n = slice(half * 512, (half + 1) * 512)
                    dve.wait_ge(sgate_ready, 2 * i + half + 1)
                    link(nc.vector.tensor_tensor(sgate[i % 2][:, n], sgate[i % 2][:, n], pp[:, i, n], ALU.mult))
                    nc.vector.tensor_tensor(xrow[:, i, n], xrow[:, i, n], sgate[i % 2][:, n], ALU.add
                                            ).then_inc(out_ready, 1)

            dve.wait_ge(ple_ready, NT)
            for i in range(NT):
                third_rows(i)
                if i:
                    third_T(i - 1)
            third_T(NT - 1)
            for i in range(NT):
                result(i)

        @block.tensor
        def _(pe):
            mm = nc.tensor.matmul

            def loaded(u):
                u = DENSE_AT[u]
                pe.wait_ge(slot_loaded[DENSE_SLOT[u]], 16 * (uses_before(DENSE_SLOT[u], u) + 1))

            def strided_T(src, i, b0, width, done):
                v = src.rearrange("p (q k) -> p k q", k=KD)
                for half in range(2):
                    for k in range(4):
                        last = nc.tensor.transpose(bank(b0 + half)[:, k * width:(k + 1) * width],
                                                   v[0:width, 4 * half + k, :], ident[0:width, 0:width])
                    last.then_inc(done, 1)

            pe.wait_ge(cst_loaded, 16)
            for i in range(NT):
                pe.wait_ge(rows_ready, i + 1)
                strided_T(rows[:, i, :], i, 2 * i, P, hT_ps)

            qv = pair_view(DENSE_SLOT[DENSE_AT["q0"]])
            kvv = unit_view(DENSE_SLOT[DENSE_AT["kv"]], KD)

            def qkv(i):
                pe.wait_ge(hT_ready, 2 * i + 2)
                if i == 0:
                    loaded("q0")
                    loaded("q1")
                if i == 1:
                    pe.wait_ge(hT_ready, 4)
                if i >= 2:
                    pe.wait_ge(q_copied, i - 1)
                    pe.wait_ge(kv_copied, i - 1)
                for k in range(KD):
                    last = mm(bank(2 * (i % 2)), actT[:, k, i * P:(i + 1) * P], qv[:, k], start=(k == 0),
                              stop=(k == KD - 1))
                last.then_inc(qkv_ps, 1)
                if i == 0:
                    loaded("kv")
                for k in range(KD):
                    last = mm(bank(2 * (i % 2) + 1)[:, 0:256], actT[:, k, i * P:(i + 1) * P], kvv[:, k],
                              start=(k == 0), stop=(k == KD - 1))
                last.then_inc(qkv_ps, 1)

            def qk_T(i):
                pe.wait_ge(qk_normed, i + 1)
                pe.wait_ge(hT_ready, 2 * NT)
                b = 4 + 2 * (i % 2)
                if i == 1:
                    pe.wait_ge(vec_ready, 1)
                if i >= 2:
                    pe.wait_ge(qkT_ready, i - 1)
                for a in range(4):
                    nc.tensor.transpose(bank(b)[:, a * P:(a + 1) * P], rows[:, i, a * P:(a + 1) * P], ident)
                for a in range(2):
                    last = nc.tensor.transpose(bank(b + 1)[:, a * P:(a + 1) * P],
                                               rows[:, i, 768 + a * P:768 + (a + 1) * P], ident)
                last.then_inc(qkT_ps, 1)

            for i in range(NT):
                qkv(i)
                if i:
                    qk_T(i - 1)
                if i == 1:
                    pe.wait_ge(small_loaded, 16 * 9)
                    nc.tensor.transpose(bank(7)[:, 0:NVEC], vecs[:, :], ident[0:NVEC, 0:NVEC]).then_inc(vec_ps, 1)
            for g in range(NG):
                u = f"pool{g // 2}"
                loaded(u)
                w = unit_view(DENSE_SLOT[DENSE_AT[u]], KD)
                pe.wait_ge(q_copied, NT)
                pe.wait_ge(kv_copied, NT)
                for k in range(KD):
                    last = mm(bank(g), w[:, k, (g % 2) * P:(g % 2 + 1) * P], actT[:, k, :], start=(k == 0),
                              stop=(k == KD - 1))
                last.then_inc(pool_ps, 1)
                if g == 1:
                    qk_T(NT - 1)

            def gate_tile(m):
                u = f"gate{m // 2}"
                loaded(u)
                w = unit_view(DENSE_SLOT[DENSE_AT[u]], KD)
                if m < 2:
                    pe.wait_ge(upool_ready, m + 1)
                else:
                    pe.wait_ge(gate_copied, m - 1)
                for k in range(KD):
                    last = mm(bank(m % 2), w[:, k, (m % 2) * P:(m % 2 + 1) * P], actT[:, k, :], start=(k == 0),
                              stop=(k == KD - 1))
                last.then_inc(gate_ps, 1)

            def scores(n):
                pe.wait_ge(qkT_ready, NT)
                if n:
                    pe.wait_ge(score_read, 4 * n)
                else:
                    pe.wait_ge(upool_ready, NG)
                o = P if n == 0 else 0
                for kv in range(NKV):
                    for par in range(2):
                        b = kv * 2 + par
                        for half in range(2):
                            last = mm(bank(2 + b)[:, half * 256 + o:half * 256 + 256],
                                      qT[64 * par:64 * par + 64, kv * 2 + half, n * P:(n + 1) * P],
                                      kT[64 * par:64 * par + 64, kv, n * P - P + o:(n + 1) * P],
                                      start=True, stop=True)
                        last.then_inc(score_ps, 1)

            def probs_T(n):
                pe.wait_ge(prob_ready, n + 1)
                for b in range(4):
                    if n == 0 and b < 2:
                        pe.wait_ge(qkT_ready, NT)
                    elif b < 2:
                        pe.wait_ge(attn_ready, n)
                    else:
                        pe.wait_ge(probT_ready, 4 * n + b - 1)
                    for kb in range(1 if n == 0 else 0, 2):
                        for half in range(2):
                            last = nc.tensor.transpose(
                                bank(6 + b % 2)[:, kb * 256 + half * P:kb * 256 + (half + 1) * P],
                                score[:, 2 * b + half, kb * P:(kb + 1) * P], ident)
                    last.then_inc(probT_ps, 1)

            def attend(n):
                pe.wait_ge(probT_ready, 4 * n + 4)
                first = 1 if n == 0 else 0
                for kv in range(NKV):
                    for par in range(2):
                        b = kv * 2 + par
                        for kb in range(first, 2):
                            last = mm(bank(6)[64 * par:64 * par + 64, kv * 256:(kv + 1) * 256],
                                      rows[:, n - 1 + kb, QD + KVD + kv * DH:QD + KVD + (kv + 1) * DH],
                                      probT[:, b, kb * 256:(kb + 1) * 256], start=(kb == first), stop=(kb == 1))
                last.then_inc(attn_ps, 1)

            def mix():
                for g in range(NG):
                    pe.wait_ge(pooled_ready, g + 1)
                    pe.wait_ge(score_read, 4 * NT)
                    mm(bank(2 + g), mixw[:, g, :], pooled[:, g, :], start=True, stop=True).then_inc(mix_ps, 1)

            scores(0)
            gate_tile(0)
            gate_tile(1)
            for n in range(NT):
                probs_T(n)
                if n + 1 < NT:
                    scores(n + 1)
                gate_tile(2 + 2 * n)
                attend(n)
                gate_tile(3 + 2 * n)
            for m in range(10, 14):
                gate_tile(m)
            mix()
            gate_tile(14)
            gate_tile(15)

            for hf in range(2):
                loaded(f"wa{hf}")
                loaded(f"wb{hf}")
                wa = unit_view(DENSE_SLOT[DENSE_AT[f"wa{hf}"]], 4)
                wb = unit_view(DENSE_SLOT[DENSE_AT[f"wb{hf}"]], 4)
                for mi in range(4):
                    m = hf * 4 + mi
                    b = 2 + 2 * (m % 2)
                    pe.wait_ge(mixed_ready, NG)
                    pe.wait_ge(attn_ready, NT)
                    if m >= 2:
                        pe.wait_ge(merged_ready, m - 1)
                    for k in range(4):
                        mm(bank(b), wa[:, k, mi * P:(mi + 1) * P], mixedT[:, k, :], start=(k == 0), stop=(k == 3))
                    for k in range(4):
                        last = mm(bank(b + 1), wb[:, k, mi * P:(mi + 1) * P], qT[:, k, :], start=(k == 0),
                                  stop=(k == 3))
                    last.then_inc(branch_ps, 1)

            def out_proj(i):
                pe.wait_ge(merged_ready, KD)
                pe.wait_ge(gate_copied, 2 * KD)
                for half in range(2):
                    if i == 0:
                        loaded(f"out{2 * half}")
                        loaded(f"out{2 * half + 1}")
                    else:
                        pe.wait_ge(x1_ready, 2 * i - 1 + half)
                    w = pair_view(DENSE_SLOT[DENSE_AT[f"out{2 * half}"]])
                    for k in range(KD):
                        last = mm(bank(half), gates[:, k, i * P:(i + 1) * P], w[:, k], start=(k == 0),
                                  stop=(k == KD - 1))
                    last.then_inc(x1_ps, 1)

            def second_T(i):
                pe.wait_ge(h2_ready, i + 1)
                if i >= 2:
                    pe.wait_ge(h2T_ready, 2 * i - 2)
                strided_T(rows[:, i, :], i, 2 + 2 * (i % 2), P, h2T_ps)

            out_proj(0)
            out_proj(1)
            out_proj(2)
            second_T(0)
            out_proj(3)
            second_T(1)
            pe.wait_ge(p_loaded, 16)
            for j in range(2):
                for i in range(NT):
                    last = nc.tensor.transpose(bank(6 + j)[:, i * P:(i + 1) * P], prow[:, i, j * P:(j + 1) * P],
                                               ident)
                last.then_inc(pT_ps, 1)
            second_T(2)

            def ple_proj(i):
                b = 2 if i % 2 == 0 else 4
                if i == 0:
                    pe.wait_ge(pT_ready, 2)
                    loaded("ple")
                if i < 2:
                    pe.wait_ge(h2T_ready, 2 * NT if i else 2 * NT - 2)
                else:
                    pe.wait_ge(ple_copied, i - 1)
                w = unit_view(DENSE_SLOT[DENSE_AT["ple"]], 2)
                for half in range(2):
                    for j in range(2):
                        last = mm(bank(b + half), pT[:, j, i * P:(i + 1) * P],
                                  w[:, j, half * 512:(half + 1) * 512], start=(j == 0), stop=(j == 1))
                last.then_inc(ple_ps, 1)

            second_T(3)
            ple_proj(0)
            pe.wait_ge(rw_loaded, 16)
            pe.wait_ge(h2T_ready, 2 * NT)
            pe.wait_ge(x1_ready, 2 * NT)
            for k in range(KD):
                last = mm(ps[0:NE, 0:T], rw[:, k, :], actT[:, k, :], start=(k == 0), stop=(k == KD - 1))
            last.then_inc(logit_ps, 1)
            ple_proj(1)
            pe.wait_ge(logit_copied, 1)
            for i in range(NT):
                last = nc.tensor.transpose(bank(1)[:, i * NE:(i + 1) * NE], r_lt[:, i * P:(i + 1) * P],
                                           ident[0:NE, 0:NE])
            last.then_inc(logitT_ps, 1)
            ple_proj(2)
            ple_proj(3)

            def shared_up(f, n):
                u = ("shg", "shu")[n]
                if f == 0:
                    loaded(u)
                pe.wait_ge(ple_copied, NT - 1 + f)
                w = unit_view(DENSE_SLOT[DENSE_AT[u]], KD)
                for k in range(KD):
                    last = mm(bank(2 + 2 * f + n), w[:, k, f * P:(f + 1) * P], actT[:, k, :], start=(k == 0),
                              stop=(k == KD - 1))
                if n == 1:
                    last.then_inc(shared_ps, 1)

            def shared_down(i):
                b = 2 + 2 * (i % 2)
                if i == 0:
                    loaded("shd")
                    pe.wait_ge(shared_act, 2)
                if i >= 2:
                    pe.wait_ge(base_ready, 2 * i - 2)
                w = unit_view(DENSE_SLOT[DENSE_AT["shd"]], 2)
                for half in range(2):
                    for j in range(2):
                        last = mm(bank(b + half), sh_act[:, j, i * P:(i + 1) * P],
                                  w[:, j, half * 512:(half + 1) * 512], start=(j == 0), stop=(j == 1))
                    last.then_inc(shdown_ps, 1)

            def lists(c):
                pe.wait_ge(place_ready, NT * (c + 1))
                if c == 0:
                    pe.wait_ge(tokcol_ready, 1)
                    pe.wait_ge(pT_ready, 2)
                for e in range(CHUNK):
                    ee = c * CHUNK + e
                    for i in range(NT):
                        last = mm(bank(6)[0:CAP, ee * LCOL:(ee + 1) * LCOL], place[:, c % 2, i, e, :],
                                  tokcol[:, i, ee, :], start=(i == 0), stop=(i == NT - 1))
                last.then_inc(place_used, 1)

            shared_up(0, 0)
            shared_up(0, 1)
            pe.wait_ge(sel_ready, 1)
            pe.wait_ge(scores_ready, 1)
            for i in range(NT):
                for q in range(i):
                    mm(bank(1)[:, i * NE:(i + 1) * NE], oneT[:, :], selb[:, q * NE:(q + 1) * NE], start=(q == 0),
                       stop=False)
                mm(bank(1)[:, i * NE:(i + 1) * NE], triT[:, :], selb[:, i * NE:(i + 1) * NE], start=(i == 0),
                   stop=True)
            for q in range(NT):
                last = mm(bank(1)[:, NR:NR + NE], oneT[:, :], selb[:, q * NE:(q + 1) * NE], start=(q == 0),
                          stop=(q == NT - 1))
            last.then_inc(rank_ps, 1)
            shared_up(1, 0)
            lists(0)
            shared_up(1, 1)
            lists(1)
            lists(2)
            for i in range(NT - 1):
                shared_down(i)
                lists(3 + i)
            lists(6)
            lists(7)
            shared_down(NT - 1)

            def rows_T(e, g, j, turn):
                pe.wait_ge(gathered[j % UNROLL], g)
                if turn is not None:
                    pe.wait_ge(hgT_lo_ready, e)
                    pe.wait_ge(hgT_hi_ready, e)
                strided_T(hg[j % UNROLL], None, 0, CAP, hgT_ps)

            def up(e, j, uses):
                s = EXPERT_SLOT[j % UNROLL]
                k = j % 2
                pe.wait_ge(slot_loaded[s], uses(s))
                pe.wait_ge(slot_loaded[s + 1], uses(s + 1))
                pe.wait_ge(hgT_lo_ready, e + 1)
                pe.wait_ge(hgT_hi_ready, e + 1)
                w = pair_view(s)
                for q in range(KD):
                    last = mm(bank(2 + k)[0:CAP, :], hgT[k][:, q, :], w[:, q], start=(q == 0), stop=(q == KD - 1))
                last.then_inc(gu_ps, 1)

            def acts_T(e, j):
                k = j % 2
                pe.wait_ge(eact_ready, e + 1)
                v = eact[k][0:CAP, :].rearrange("p (q j) -> p j q", j=2)
                for q in range(2):
                    last = nc.tensor.transpose(bank(4)[:, q * CAP:(q + 1) * CAP], v[:, q, :], ident[0:CAP, 0:CAP])
                last.then_inc(eactT_ps, 1)

            def down(e, j, uses, first=False):
                s = EXPERT_SLOT[j % UNROLL] + 2
                k = j % 2
                pe.wait_ge(slot_loaded[s], uses(s))
                pe.wait_ge(eactT_ready, e + 1)
                if not first:
                    pe.wait_ge(y_ready, e)
                w = unit_view(s, 2)
                for half in range(2):
                    for q in range(2):
                        last = mm(bank(6 + half)[0:CAP, :], eactT[k][:, q, :], w[:, q, half * 512:(half + 1) * 512],
                                  start=(q == 0), stop=(q == 1))
                last.then_inc(y_ps, 1)

            pe.wait_ge(list_ready, 1)
            pe.wait_ge(base_ready, 2 * NT)
            rows_T(0, 16, 0, None)

            def static_uses(turn):
                return lambda s: 16 * (USES[s] + turn + 1)

            def step(e, j, uses, prev_uses, turn, g_next, first=False, second=False, last=False):
                up(e, j, uses)
                if not first:
                    acts_T(e - 1, j - 1)
                if not last:
                    rows_T(e + 1, g_next, j + 1, 0)
                if not first:
                    down(e - 1, (j - 1) % UNROLL, prev_uses, first=second)

            def static_step(e):
                step(e, e % UNROLL, static_uses(e // UNROLL), static_uses((e - 1) // UNROLL), 0,
                     16 * ((e + 1) // UNROLL + 1), first=(e == 0), second=(e == 1), last=(e == NE - 1))

            for e in range(UNROLL):
                static_step(e)
            with pe.Fori(1, TURNS - 1) as turn:
                for j in range(UNROLL):
                    e = turn * UNROLL + j

                    def uses(s):
                        return (turn + (USES[s] + 1)) * 16

                    def prev_uses(s):
                        return (turn + (USES[s] + (0 if j == 0 else 1))) * 16

                    g_next = (turn + ((j + 1) // UNROLL + 1)) * 16
                    step(e, j, uses, prev_uses, turn, g_next)
            for e in range(NE - UNROLL, NE):
                static_step(e)
            acts_T(NE - 1, (NE - 1) % UNROLL)
            down(NE - 1, (NE - 1) % UNROLL, static_uses(TURNS - 1))

            def o_start(j):
                pe.wait_ge(added, 16 * NE)

            def o_products(e, n, j):
                pe.wait_ge(o_over, n + 1)
                pe.wait_ge(o_place_ready, n + 1)
                for i in range(NT):
                    last = mm(bank(5)[0:CAP, 0:LCOL], o_place[:, i, :],
                              tokcol[:, i, bass.ds(e, 1), :].rearrange("p e c -> p (e c)"),
                              start=(i == 0), stop=(i == NT - 1))
                last.then_inc(o_list_ps, 1)
                pe.wait_ge(o_gathered, 16 * (n + 1))
                strided_T(hg[0], None, 0, CAP, o_hgT_ps)
                pe.wait_ge(o_hgT_lo, n + 1)
                pe.wait_ge(o_hgT_hi, n + 1)
                pe.wait_ge(o_loaded[0], 16 * (n + 1))
                pe.wait_ge(o_loaded[1], 16 * (n + 1))
                w = pair_view(O_SLOT)
                for q in range(KD):
                    last = mm(bank(2)[0:CAP, :], hgT[0][:, q, :], w[:, q], start=(q == 0), stop=(q == KD - 1))
                last.then_inc(o_gu_ps, 1)
                pe.wait_ge(o_act, n + 1)
                v = eact[0][0:CAP, :].rearrange("p (q j) -> p j q", j=2)
                for q in range(2):
                    last = nc.tensor.transpose(bank(4)[:, q * CAP:(q + 1) * CAP], v[:, q, :], ident[0:CAP, 0:CAP])
                last.then_inc(o_actT_ps, 1)
                pe.wait_ge(o_actT, n + 1)
                pe.wait_ge(o_loaded[2], 16 * (n + 1))
                w = unit_view(O_SLOT + 2, 2)
                for half in range(2):
                    for q in range(2):
                        last = mm(bank(6 + half)[0:CAP, :], eactT[0][:, q, :],
                                  w[:, q, half * 512:(half + 1) * 512], start=(q == 0), stop=(q == 1))
                last.then_inc(o_y_ps, 1)

            further_rounds(pe, o_start, o_products)

            def third_T(i):
                pe.wait_ge(rows3_ready, i + 1)
                if i >= 2:
                    pe.wait_ge(h3T_ready, 2 * i - 2)
                strided_T(rows[:, i, :], i, 2 + 2 * (i % 2), P, h3T_ps)

            def ple_gate_tile(i):
                pe.wait_ge(h3T_ready, 2 * i + 2)
                for half in range(2):
                    if i:
                        pe.wait_ge(sgate_ready, 2 * i - 1 + half)
                    for c in range(2):
                        s = TAIL_SLOT[2 * half + c]
                        if i == 0:
                            pe.wait_ge(slot_loaded[s], 16 * (USES[s] + TURNS + 1))
                        w = unit_view(s, KD)
                        for k in range(KD):
                            last = mm(bank(half)[:, c * 256:(c + 1) * 256], actT[:, k, i * P:(i + 1) * P], w[:, k],
                                      start=(k == 0), stop=(k == KD - 1))
                    last.then_inc(final_ps, 1)

            for i in range(NT):
                third_T(i)
                if i:
                    ple_gate_tile(i - 1)
            ple_gate_tile(NT - 1)


_INS = ["x", "p", "g_mix", "w_in", "w_pool_mix", "pool_scale", "w_branch_a", "q_gain", "k_gain", "attn_sinks",
        "w_branch_b", "w_gate", "b_gate", "w_out", "g_ffn", "w_router", "router_bias", "w_exp_gate", "w_exp_up",
        "w_exp_down", "w_sh_gate", "w_sh_up", "w_sh_down", "g_ple", "w_ple_gate", "w_ple_proj", "g_ple_post"]


def program(nc, args, out):
    h2 = nc.dram_tensor("h2_rows", (T, D), F32, kind="Internal").ap()
    acc = nc.dram_tensor("accumulator", (ACC_ROWS, D), F32, kind="Internal").ap()
    build(nc, args, acc, h2, out)


def kernel(**inputs):
    import concourse.bacc as _bacc
    from concourse.bass_utils import run_bass_kernel_spmd as _run

    nc = _bacc.Bacc("TRN2", target_bir_lowering=False, num_devices=1)
    arrays, args = {}, {}
    data = {name: np.ascontiguousarray(inputs[name]) for name in _INS}
    data["constants"] = constant_table()
    data["alibi"] = alibi_table()
    for name, a in data.items():
        arrays[f"in_{name}"] = a
        args[name] = nc.dram_tensor(f"in_{name}", a.shape, mybir.dt.from_np(a.dtype), kind="ExternalInput").ap()
    out = nc.dram_tensor("out", data["x"].shape, F32, kind="ExternalOutput").ap()
    program(nc, args, out)
    r = _run(nc, [arrays], core_ids=[0])
    return r.results[0]["out"]
```
